# Optimizing a Trainium2 kernel written in Bass

```python
import math
import jax, jax.numpy as jnp
from jax import lax
import numpy as np

D_MODEL = 2048
BATCH = 1
SEQ = 256
DEPTH = 1

MIX_WIDTH = D_MODEL
CONV_WIDTH = MIX_WIDTH // 2
CONV_GROUPS = 8
CONV_K = 3
ATTN_WIDTH = MIX_WIDTH - CONV_WIDTH
N_DIFF_HEADS = 8
DIFF_DK = ATTN_WIDTH // N_DIFF_HEADS // 2
DIFF_DV = 2 * DIFF_DK
FFN_DIM = 5632
Q_BLOCK = 128
EPS = 1e-6
IN_COLS = 3 * CONV_WIDTH + 3 * ATTN_WIDTH

kernel_name = "hybrid_conv_diffattn_macaron_block"

def rms_norm(x, g):
    xf = x.astype(jnp.float32)
    y = xf * lax.rsqrt(jnp.mean(xf * xf, axis=-1, keepdims=True) + EPS)
    return (y * g.astype(jnp.float32)).astype(x.dtype)

def swiglu(x, w_gate, w_up, w_down):
    return (jax.nn.silu(x @ w_gate) * (x @ w_up)) @ w_down

def causal_depthwise_conv(u, w):
    s = u.shape[1]
    u_pad = jnp.pad(u, ((0, 0), (CONV_K - 1, 0), (0, 0)))
    return sum(w[k] * u_pad[:, k:k + s] for k in range(CONV_K))

def short_conv_mixer(b_gate, c_gate, xv, conv_w):
    return b_gate * causal_depthwise_conv(c_gate * xv, conv_w)

def diff_attention(q, k, v, lam):
    bsz, s = q.shape[0], q.shape[1]
    nb = s // Q_BLOCK
    scale = 1.0 / math.sqrt(DIFF_DK)
    qb = q.reshape(bsz, nb, Q_BLOCK, N_DIFF_HEADS, 2, DIFF_DK).transpose(1, 0, 3, 4, 2, 5)
    kt = k.transpose(0, 2, 3, 1, 4)
    vt = v.transpose(0, 2, 1, 3)
    key_pos = jnp.arange(s)

    def block(args):
        q_blk, i = args
        scores = jnp.einsum('bhcqd,bhckd->bhcqk', q_blk, kt).astype(jnp.float32) * scale
        q_pos = i * Q_BLOCK + jnp.arange(Q_BLOCK)
        mask = key_pos[None, :] <= q_pos[:, None]
        scores = jnp.where(mask, scores, -jnp.inf)
        p = jax.nn.softmax(scores, axis=-1)
        a = p[:, :, 0] - lam * p[:, :, 1]
        return jnp.einsum('bhqk,bhkd->bhqd', a.astype(vt.dtype), vt)

    o = lax.map(block, (qb, jnp.arange(nb)))
    return o.transpose(1, 0, 3, 2, 4).reshape(bsz, s, N_DIFF_HEADS, DIFF_DV)

def setup_inputs(seed: int = 0) -> dict:
    key = jax.random.key(seed)
    ks = jax.random.split(key, 20)
    f32 = jnp.float32

    def w(k, shape, fan_in):
        return jax.random.normal(k, shape, f32) * fan_in ** -0.5

    def gain(k, shape):
        return 1.0 + 0.05 * jax.random.normal(k, shape, f32)

    return {
        "x": jax.random.normal(ks[0], (BATCH, SEQ, D_MODEL), f32),
        "ffn1_norm": gain(ks[1], (DEPTH, D_MODEL)),
        "ffn1_w_gate": w(ks[2], (DEPTH, D_MODEL, FFN_DIM), D_MODEL),
        "ffn1_w_up": w(ks[3], (DEPTH, D_MODEL, FFN_DIM), D_MODEL),
        "ffn1_w_down": w(ks[4], (DEPTH, FFN_DIM, D_MODEL), FFN_DIM),
        "mix_norm": gain(ks[5], (DEPTH, D_MODEL)),
        "w_in": w(ks[6], (DEPTH, D_MODEL, IN_COLS), D_MODEL),
        "conv_w": w(ks[7], (DEPTH, CONV_K, CONV_WIDTH), CONV_K),
        "lambda_q1": 0.1 * jax.random.normal(ks[8], (DEPTH, DIFF_DK), f32),
        "lambda_k1": 0.1 * jax.random.normal(ks[9], (DEPTH, DIFF_DK), f32),
        "lambda_q2": 0.1 * jax.random.normal(ks[10], (DEPTH, DIFF_DK), f32),
        "lambda_k2": 0.1 * jax.random.normal(ks[11], (DEPTH, DIFF_DK), f32),
        "subln_w": gain(ks[12], (DEPTH, DIFF_DV)),
        "w_out": w(ks[13], (DEPTH, MIX_WIDTH, D_MODEL), MIX_WIDTH),
        "ffn2_norm": gain(ks[14], (DEPTH, D_MODEL)),
        "ffn2_w_gate": w(ks[15], (DEPTH, D_MODEL, FFN_DIM), D_MODEL),
        "ffn2_w_up": w(ks[16], (DEPTH, D_MODEL, FFN_DIM), D_MODEL),
        "ffn2_w_down": w(ks[17], (DEPTH, FFN_DIM, D_MODEL), FFN_DIM),
        "final_norm": gain(ks[18], (D_MODEL,)),
    }

def reference(x, ffn1_norm, ffn1_w_gate, ffn1_w_up, ffn1_w_down, mix_norm, w_in,
              conv_w, lambda_q1, lambda_k1, lambda_q2, lambda_k2, subln_w, w_out,
              ffn2_norm, ffn2_w_gate, ffn2_w_up, ffn2_w_down, final_norm):
    bsz, s, _ = x.shape
    for l in range(DEPTH):
        x = x + 0.5 * swiglu(rms_norm(x, ffn1_norm[l]), ffn1_w_gate[l], ffn1_w_up[l], ffn1_w_down[l])

        h = rms_norm(x, mix_norm[l])
        proj = h @ w_in[l]
        b_gate, c_gate, xv, q, k, v = jnp.split(
            proj, np.cumsum([CONV_WIDTH] * 3 + [ATTN_WIDTH] * 2).tolist(), axis=-1)

        y_conv = short_conv_mixer(b_gate, c_gate, xv, conv_w[l])

        lambda_init = 0.8 - 0.6 * math.exp(-0.3 * l)
        lam = (jnp.exp(jnp.sum(lambda_q1[l].astype(jnp.float32) * lambda_k1[l].astype(jnp.float32)))
               - jnp.exp(jnp.sum(lambda_q2[l].astype(jnp.float32) * lambda_k2[l].astype(jnp.float32)))
               + lambda_init)
        q = q.reshape(bsz, s, N_DIFF_HEADS, 2, DIFF_DK)
        k = k.reshape(bsz, s, N_DIFF_HEADS, 2, DIFF_DK)
        v = v.reshape(bsz, s, N_DIFF_HEADS, DIFF_DV)
        o = diff_attention(q, k, v, lam)
        o = rms_norm(o, subln_w[l]) * (1.0 - lambda_init)
        y_attn = o.reshape(bsz, s, ATTN_WIDTH)

        x = x + jnp.concatenate([y_conv, y_attn], axis=-1) @ w_out[l]

        x = x + 0.5 * swiglu(rms_norm(x, ffn2_norm[l]), ffn2_w_gate[l], ffn2_w_up[l], ffn2_w_down[l])

    return rms_norm(x, final_norm)


_drawn_inputs = setup_inputs


def setup_inputs(seed=0):
    import zlib

    import numpy as np

    out = dict(_drawn_inputs(seed))
    spreads = {}
    factors = {'lambda_k1': 8.0, 'lambda_q2': 8.0, 'subln_w': 2.925, 'ffn2_norm': 3.661}
    for name, (base, spread) in spreads.items():
        noise = np.random.default_rng([zlib.crc32(name.encode()), seed]).standard_normal(out[name].shape)
        drawn = base * np.exp(spread * noise) if base else spread * noise
        out[name] = __import__('jax').numpy.asarray(drawn.astype(out[name].dtype))
    for name, factor in factors.items():
        out[name] = (out[name] * factor).astype(out[name].dtype)
    return out
```

```python
import concourse.bass as bass
from concourse import mybir
from contextlib import ExitStack

F32 = mybir.dt.float32
F32R = mybir.dt.float32r
I32 = mybir.dt.int32
ALU = mybir.AluOpType
ACT = mybir.ActivationFunctionType

P = 128
D = 2048
SEQ = 256
TT = SEQ // P
FFN = 5632
HEADS = 8
DV = 128
DK = 64
KD = D // P
KF = FFN // P
W = 512
KC = 2
RING = 4
CD = KD // KC
CF = KF // KC
GROUPS = FFN // W
XG = D // W
BT = W // P
HALF = 1024
J = HALF // W
HJ = W // DV
EPS = 1e-6
LAMBDA_INIT = 0.8 - 0.6
SCALE = DK ** -0.5
MASKED = -1e30
LOWEST = -3e38
MAGIC = float(0x5F3759DF)
NEWTON = 3

Q, K, V, B, C, X = range(6)
PART = {Q: 3 * HALF, K: 4 * HALF, V: 5 * HALF, B: 0, C: HALF, X: 2 * HALF}
OUT_ORDER = [4, 5, 6, 7, 0, 1, 2, 3]

CH_FFN1 = 0
CH_DOWN1 = CH_FFN1 + GROUPS * 2 * CD
CH_MIX = CH_DOWN1 + XG * CF
CH_OUT = CH_MIX + J * 6 * CD
CH_FFN2 = CH_OUT + XG * CD
CH_DOWN2 = CH_FFN2 + GROUPS * 2 * CD
CH_END = CH_DOWN2 + XG * CF
PR_FFN1 = 0
PR_DOWN1 = PR_FFN1 + GROUPS
PR_MIX = PR_DOWN1 + XG // 2
PR_OUT = PR_MIX + 3 * J
PR_FFN2 = PR_OUT + XG // 2
PR_DOWN2 = PR_FFN2 + GROUPS
TB_X1 = 0
TB_H1 = TB_X1 + 2 * XG
TB_XM = TB_H1 + 2 * GROUPS
TB_HEAD = TB_XM + 2 * XG
TB_X2 = TB_HEAD + HEADS
TB_H2 = TB_X2 + 2 * XG
COL_G1, COL_GM, COL_G2, COL_SUB, COL_CONV = 0, KD, 2 * KD, 3 * KD, 3 * KD + 1
COLS = COL_CONV + 3 * (HALF // P)


class Steps:

    def __init__(self, eng, sem):
        self.eng, self.sem, self.base, self.n = eng, sem, 0, 0

    def link(self, ins):
        self.n += 1
        ins.then_inc(self.sem, 1)
        self.eng.wait_ge(self.sem, self.base + self.n)

    def enter(self, i, each):
        self.outer, self.each, self.base, self.n = self.base + self.n, each, self.base + self.n + i * each, 0

    def leave(self, times):
        assert self.n == self.each, (self.n, self.each)
        self.base, self.n = self.outer + times * self.each, 0


def hybrid_block(nc, x_in, wg1, wu1, wd1, w_in, w_out, wg2, wu2, wd2, gf, columns, lambdas, out):
    ctx = ExitStack()
    with ctx:
        def sb(name, shape, dt=F32):
            return ctx.enter_context(nc.sbuf_tensor(name, shape, dt))

        def sem(name):
            return ctx.enter_context(nc.semaphore(name))

        raw = [sb(f"raw{i}", [P, KC, W]) for i in range(RING)]
        w_hi = [sb(f"w_hi{i}", [P, KC, W], F32R) for i in range(RING)]
        w_lo = [sb(f"w_lo{i}", [P, KC, W], F32R) for i in range(RING)]
        x = sb("x", [P, TT, D])
        xT_hi = sb("xT_hi", [P, KD, SEQ], F32R)
        xT_lo = sb("xT_lo", [P, KD, SEQ], F32R)
        gate = sb("gate", [P, TT, W])
        turn_in = sb("turn_in", [P, TT, W])
        gfin = sb("gfin", [P, D])
        spare = sb("spare", [P, 1])
        ident = sb("ident", [P, P])
        mask = sb("mask", [P, 3 * P])
        cols = sb("cols", [P, COLS])
        gcol = sb("gcol", [P, BT])
        cw = sb("cw", [P, 3, BT])
        sub_col = sb("sub_col", [P, 1])
        neg_lam = sb("neg_lam", [P, 1])
        lam_dot = sb("lam_dot", [P, 2])
        lam_exp = sb("lam_exp", [P, 2])
        sq = sb("sq", [P, TT])
        ssum = sb("ssum", [P, TT])
        rstd = sb("rstd", [P, TT])
        osq = sb("osq", [P, TT])
        orstd = sb("orstd", [P, TT])
        nv = sb("nv", [P, TT])
        nt = sb("nt", [P, TT])
        rowmax = sb("rowmax", [P, 4])
        negmax = sb("negmax", [P, 4])
        rowsum = sb("rowsum", [P, 4])
        rinv = sb("rinv", [P, 4])
        rneg = sb("rneg", [P, 2])
        lam_rows = turn_in[:, 1, 0:4 * DK].rearrange("p (a d) -> p a d", a=4)

        with ExitStack() as region:
            def part(name, shape, dt=F32):
                return region.enter_context(nc.sbuf_tensor(name, shape, dt))
            hT_hi = part("hT_hi", [P, KF, SEQ], F32R)
            hT_lo = part("hT_lo", [P, KF, SEQ], F32R)
        yT_hi = sb("yT_hi", [P, KD, SEQ], F32R)
        yT_lo = sb("yT_lo", [P, KD, SEQ], F32R)
        part_s = {u: sb(f"part{u}", [P, TT, W]) for u in (Q, K, V, B, C)}
        upad = sb("upad", [P, BT, SEQ + 2])
        bT = sb("bT", [P, BT, SEQ])
        conv = sb("conv", [P, BT, SEQ])
        qkT = sb("qkT", [P, 2 * SEQ])
        probs = sb("probs", [P, 2, 3 * P])
        attn = sb("attn", [P, 3 * P])
        attnT = sb("attnT", [P, 3 * P])
        head = sb("head", [P, TT, DV])

        bank = [ctx.enter_context(nc.psum_tensor(f"bank{i}", [P, W], F32)) for i in range(8)]
        T_LOW, T_HIGH = (4, 5), (6, 7)

        raw_loaded = [sem(f"raw_loaded{i}") for i in range(RING)]
        x_loaded = [sem(f"x_loaded{i}") for i in range(XG)]
        cols_loaded = sem("cols_loaded")
        lam_loaded = sem("lam_loaded")
        gfin_loaded = sem("gfin_loaded")
        hi_ready = sem("hi_ready")
        lo_ready = sem("lo_ready")
        chunk_used = sem("chunk_used")
        upper_done = sem("upper_done")
        drained = [sem("drained_first"), sem("drained_second")]
        turned = sem("turned")
        turned_hi = sem("turned_hi")
        turned_lo = sem("turned_lo")
        squares_ready = sem("squares_ready")
        sums_taken = sem("sums_taken")
        rstd_ready = sem("rstd_ready")
        x_saved = sem("x_saved")
        gcol_ready = sem("gcol_ready")
        ident_ready = sem("ident_ready")
        mask_ready = sem("mask_ready")
        lam_dots = sem("lam_dots")
        lam_exps = sem("lam_exps")
        qk_turned = sem("qk_turned")
        qk_copied = sem("qk_copied")
        scores_ready = sem("scores_ready")
        masked = sem("masked")
        exps_done = sem("exps_done")
        attn_ready = sem("attn_ready")
        attn_turned = sem("attn_turned")
        attn_copied = sem("attn_copied")
        heads_ready = sem("heads_ready")
        head_squares = sem("head_squares")
        heads_scaled = sem("heads_scaled")
        conv_free = sem("conv_free")
        cw_ready = sem("cw_ready")
        conv_turned = sem("conv_turned")
        conv_copied = sem("conv_copied")
        conv_ready = sem("conv_ready")
        conv_hi = sem("conv_hi")
        conv_lo = sem("conv_lo")
        vector_step = sem("vector_step")
        pool_step = sem("pool_step")
        scaled = [sem("scaled_by_scalar"), sem("scaled_by_vector")]
        stored = sem("stored")

        block = ctx.enter_context(nc.Block())

        @block.sync
        def _(sp):
            def load(n, slot, w, pair, col):
                if not (isinstance(n, int) and n < RING):
                    sp.wait_ge(lo_ready, n - RING + 1)
                src = w[0].rearrange("(k p) n -> p k n", p=P)[:, KC * pair:KC * pair + KC, bass.ds(col, W)]
                sp.dma_start(raw[slot][:], src).then_inc(raw_loaded[slot], 16)

            def load_x(g):
                src = x_in[0].rearrange("(t p) n -> p t n", p=P)[:, :, g * W:(g + 1) * W]
                sp.dma_start(x[:, :, g * W:(g + 1) * W], src).then_inc(x_loaded[g], 16)

            def gate_up(base, wg, wu, c, first=False):
                for u, w in enumerate((wg, wu)):
                    for k in range(CD):
                        n = base + 2 * CD * c + CD * u + k
                        if first and u == 0 and k < XG:
                            load_x(k)
                        load(n, k % RING, w, k, c * W)

            def down(base, w, chunks, order):
                with sp.Fori(1, XG // 2 + 1) as i:
                    for b in range(2):
                        for k in range(chunks):
                            load(2 * chunks * i + (base + chunks * (b - 2) + k), (chunks * b + k) % RING,
                                 w, order[k], i * (2 * W) + (b - 2) * W)

            gate_up(CH_FFN1, wg1, wu1, 0, first=True)
            with sp.Fori(1, GROUPS) as c:
                gate_up(CH_FFN1, wg1, wu1, c)
            down(CH_DOWN1, wd1, CF, range(CF))
            with sp.Fori(1, J + 1) as j:
                for u in (Q, K, V, B, C, X):
                    for k in range(CD):
                        load(6 * CD * j + (CH_MIX + CD * (u - 6) + k), k % RING, w_in, k, j * W + (PART[u] - W))
            down(CH_OUT, w_out, CD, OUT_ORDER)
            with sp.Fori(0, GROUPS) as c:
                gate_up(CH_FFN2, wg2, wu2, c)
            down(CH_DOWN2, wd2, CF, range(CF))
            for g in range(XG):
                for t in range(TT):
                    sp.wait_ge(scaled[t], g + 1)
                    cs = slice(g * W, (g + 1) * W)
                    sp.dma_start(out[0, t * P:(t + 1) * P, cs], x[:, t, cs]).then_inc(stored, 16)
            sp.wait_ge(stored, 16 * XG * TT)

        @block.tensor
        def _(pe):
            def unit(base, pair, second, hi, lo, chunks, k, order=None):
                pe.wait_ge(lo_ready, base + k + 1)
                slot = ((chunks if second else 0) + k) % RING
                tile = order[k] if order else k
                for t in range(TT):
                    acc = bank[2 * second + t][:]
                    ts = slice(t * P, (t + 1) * P)
                    for kk in range(KC):
                        kt = KC * tile + kk
                        pe.matmul(acc, hi[:, kt, ts], w_hi[slot][:, kk], start=(k == 0 and kk == 0), stop=False)
                        pe.matmul(acc, hi[:, kt, ts], w_lo[slot][:, kk], start=False, stop=False)
                        mm = pe.matmul(acc, lo[:, kt, ts], w_hi[slot][:, kk], start=False,
                                       stop=(k == chunks - 1 and kk == KC - 1))
                    if k == chunks - 1 and t == 0:
                        mm.then_inc(upper_done, 1)
                mm.then_inc(chunk_used, 1)

            def banks_free(pair, second):
                if not (isinstance(pair, int) and pair == 0):
                    pe.wait_ge(drained[second], pair * TT)

            def turn(src, banks, t, done):
                for b in range(2):
                    for kk in range(2):
                        blk = 2 * b + kk
                        mm = pe.transpose(bank[banks[b]][:, kk * SEQ + t * P:kk * SEQ + (t + 1) * P],
                                          src[:, t, blk * P:(blk + 1) * P], ident[:])
                    if t == TT - 1:
                        mm.then_inc(done, 1)

            def turn_drained(tb, pair, second, banks):
                pe.wait_ge(turned_lo, tb)
                for t in range(TT):
                    pe.wait_ge(drained[second], pair * TT + t + 1)
                    turn(turn_in, banks, t, turned)

            def turn_x(g):
                if g == 0:
                    pe.wait_ge(ident_ready, 2)
                if g >= 2:
                    pe.wait_ge(turned_lo, TB_X1 + 2 * (g - 1))
                pe.wait_ge(x_loaded[g], 16)
                for t in range(TT):
                    turn(x[:, :, g * W:(g + 1) * W], T_LOW if g % 2 == 0 else T_HIGH, t, turned)

            def gate_up(ch, pr, tbx, tbh, c, first=False, start=False):
                for second in range(2):
                    banks_free(pr + c, second)
                    for k in range(CD):
                        if first and second == 0:
                            pe.wait_ge(turned_lo, tbx + k + 1)
                        unit(ch + 2 * CD * c + CD * second, pr + c, second, xT_hi, xT_lo, CD, k)
                        if start and second == 0 and k + 2 < XG:
                            turn_x(k + 2)
                        if not first and second == 0 and k == 1:
                            turn_drained(tbh + 2 * (c - 1), pr + c - 1, 1, T_LOW)

            def residual(ch, pr, tb, hi, lo, chunks, order=None, ready=None, final=False):
                with pe.Fori(0, XG // 2) as i:
                    for second in range(2):
                        banks_free(pr + i, second)
                        for k in range(chunks):
                            if second == 0:
                                ready(k)
                            unit(ch + 2 * chunks * i + chunks * second, pr + i, second, hi, lo, chunks, k, order)
                            if second == 1 and k == 1 and not final:
                                turn_drained(tb + 4 * i, pr + i, 0, T_HIGH)
                    if not final:
                        turn_drained(tb + 4 * i + 2, pr + i, 1, T_HIGH)

            def feed_forward(ch, pr, tbx, tbh, ch_down, pr_down, tb_next, start, final):
                gate_up(ch, pr, tbx, tbh, 0, first=True, start=start)
                with pe.Fori(1, GROUPS) as c:
                    gate_up(ch, pr, tbx, tbh, c)
                turn_drained(tbh + 2 * (GROUPS - 1), pr + GROUPS - 1, 1, T_LOW)

                def ready(k):
                    if k == 0:
                        pe.wait_ge(turned_lo, tbh + 2 * (GROUPS - 1))
                    if k >= CF - 2:
                        pe.wait_ge(turned_lo, tbh + k + 1)
                residual(ch_down, pr_down, tb_next, hT_hi, hT_lo, CF, ready=ready, final=final)

            def turn_qk(hb, tb, pair, h):
                if h == 0:
                    for d in drained:
                        pe.wait_ge(d, (pair + 1) * TT)
                else:
                    pe.wait_ge(turned_lo, tb + h - 1)
                for n, u in enumerate((Q, K)):
                    for t in range(TT):
                        mm = pe.transpose(bank[4][:, n * SEQ + t * P:n * SEQ + (t + 1) * P],
                                          part_s[u][:, t, h * DV:(h + 1) * DV], ident[:])
                mm.then_inc(qk_turned, 1)

            def scores(hb, h, jb):
                pe.wait_ge(qk_copied, hb + h + 1)
                if h > 0:
                    pe.wait_ge(masked, hb + h)
                if h == HJ - 1:
                    pe.wait_ge(conv_copied, jb + 2)
                for c in range(2):
                    cs = slice(c * DK, (c + 1) * DK)
                    for t in range(TT):
                        mm = pe.matmul(bank[5 + c][:, t * P:t * P + (t + 1) * P],
                                       qkT[cs, t * P:(t + 1) * P], qkT[cs, SEQ:SEQ + (t + 1) * P],
                                       start=True, stop=True)
                mm.then_inc(scores_ready, 1)

            def turn_attn(hb, h):
                pe.wait_ge(attn_ready, hb + h + 1)
                for n in range(3):
                    mm = pe.transpose(bank[7][:, n * P:(n + 1) * P], attn[:, n * P:(n + 1) * P], ident[:])
                mm.then_inc(attn_turned, 1)

            def head_out(hb, h, pair):
                pe.wait_ge(attn_copied, hb + h + 1)
                if h == 0:
                    pe.wait_ge(drained[0], (pair + 2) * TT)
                for t in range(TT):
                    for kt in range(t + 1):
                        mm = pe.matmul(bank[7][:, t * DV:(t + 1) * DV], attnT[:, (t + kt) * P:(t + kt + 1) * P],
                                       part_s[V][:, kt, h * DV:(h + 1) * DV], start=(kt == 0), stop=(kt == t))
                mm.then_inc(heads_ready, 1)

            def turn_head(hb, h):
                pe.wait_ge(heads_scaled, hb + h + 1)
                pe.wait_ge(qk_copied, hb + min(h + 2, HJ))
                for t in range(TT):
                    mm = pe.transpose(bank[4][:, t * P:(t + 1) * P], head[:, t], ident[:])
                mm.then_inc(turned, 1)

            turn_x(0)
            turn_x(1)
            feed_forward(CH_FFN1, PR_FFN1, TB_X1, TB_H1, CH_DOWN1, PR_DOWN1, TB_XM, True, False)

            with pe.Fori(0, J) as j:
                ch, pair, hb, tb, jb = CH_MIX + 6 * CD * j, PR_MIX + 3 * j, HJ * j, TB_HEAD + HJ * j, 4 * j
                for u in (Q, K, V, B, C, X):
                    banks_free(pair + u // 2, u % 2)
                    for k in range(CD):
                        if u == Q and k == 0:
                            pe.wait_ge(turned_lo, TB_XM + 2 * (XG - 1))
                        if u == Q and k >= CD - 2:
                            pe.wait_ge(turned_lo, TB_XM + k + 1)
                        unit(ch + CD * u, pair + u // 2, u % 2, xT_hi, xT_lo, CD, k)
                        s = CD * (u - B) + k
                        for h in range(HJ):
                            if s == 5 * h + 5:
                                head_out(hb, h, pair)
                            if s == 5 * h + 7:
                                turn_head(hb, h)
                            if s == 5 * h:
                                turn_qk(hb, tb, pair, h)
                            if s == 5 * h + 1:
                                scores(hb, h, jb)
                            if s == 5 * h + 4:
                                turn_attn(hb, h)
                        if s == 14:
                            pe.wait_ge(drained[1], (pair + 2) * TT)
                            pe.wait_ge(masked, hb + 3)
                            for t in range(TT):
                                turn(part_s[B], (5, 6), t, conv_turned)
                pe.wait_ge(masked, hb + HJ)
                for t in range(TT):
                    pe.wait_ge(drained[1], (pair + 2) * TT + t + 1)
                    turn(part_s[C], (5, 6), t, conv_turned)

            def ready(k):
                if k == 0:
                    pe.wait_ge(turned_lo, TB_X2)
                if k == 4:
                    pe.wait_ge(conv_lo, 1)
                if k == 6:
                    pe.wait_ge(conv_lo, 2)
            residual(CH_OUT, PR_OUT, TB_X2, yT_hi, yT_lo, CD, order=OUT_ORDER, ready=ready)
            feed_forward(CH_FFN2, PR_FFN2, TB_X2, TB_H2, CH_DOWN2, PR_DOWN2, None, False, True)

        @block.scalar
        def _(act):
            def high(m, slot):
                act.wait_ge(raw_loaded[slot], ring_count(m, slot))
                if not (isinstance(m, int) and m < RING):
                    act.wait_ge(chunk_used, m - RING + 1)
                act.activation(w_hi[slot][:], raw[slot][:], ACT.Copy).then_inc(hi_ready, 1)

            def split_x(tb, banks, gain, hi, k0):
                for b in range(2):
                    act.wait_ge(turned, tb + b + 1)
                    for kk in range(2):
                        blk = 2 * b + kk
                        a = act.activation(hi[:, bass.ds(k0 + blk, 1), :].rearrange("p a n -> p (a n)"),
                                           bank[banks[b]][:, kk * SEQ:(kk + 1) * SEQ],
                                           ACT.Copy, scale=gain[:, blk:blk + 1])
                    a.then_inc(turned_hi, 1)

            def split_hidden(tb, c):
                for b in range(2):
                    act.wait_ge(turned, tb + b + 1)
                    act.activation(hT_hi[:, bass.ds(BT * c + 2 * b, 2), :],
                                   bank[T_LOW[b]][:].rearrange("p (a n) -> p a n", a=2), ACT.Copy)\
                       .then_inc(turned_hi, 1)

            def squares(src, q, waits):
                if not (isinstance(q, int) and q == 0):
                    act.wait_ge(sums_taken, q)
                for t in range(TT):
                    waits(t)
                    a = act.activation(gate[:, t], src[:, t], ACT.Square, accum_out=sq[:, t:t + 1])
                a.then_inc(squares_ready, 1)

            def unit_done(ch_end, pair, second, t):
                if t == 0:
                    act.wait_ge(upper_done, pair * 2 + second + 1)
                else:
                    act.wait_ge(chunk_used, ch_end)

            def gate_up(ch, pr, tbh, norm, c, first=False, start=False):
                base = ch + 2 * CD * c
                for n in range(2 * CD):
                    if n == CD - 1:
                        if first:
                            act.wait_ge(rstd_ready, norm)
                        if not (isinstance(c, int) and c + pr == 0):
                            act.wait_ge(drained[1], (pr + c) * TT)
                        for t in range(TT):
                            unit_done(base + CD, pr + c, 0, t)
                            act.activation(gate[:, t], bank[t][:], ACT.Silu, scale=rstd[:, t:t + 1])\
                               .then_inc(drained[0], 1)
                    high(base + n + RING, n % RING)
                    if start and 2 <= n < 2 + XG:
                        g = n - 2
                        squares(x[:, :, g * W:(g + 1) * W], g, lambda t: None)
                    if not first and n == 1:
                        split_hidden(tbh + 2 * (c - 1), c - 1)

            def residual(ch, pr, tb, q, r, chunks, final, i, last=False):
                for second in range(2):
                    g = i * 2 + second
                    for k in range(chunks):
                        if not (last and second == 1 and k >= chunks - RING):
                            high(ch + 2 * chunks * i + chunks * second + k + RING, (chunks * second + k) % RING)
                        if second == 1 and k == 1 and not final:
                            act.wait_ge(gcol_ready, r + i * 2 + 1)
                            split_x(tb + 4 * i, T_HIGH, gcol, xT_hi, i * 8)
                    squares(turn_in, q + g, lambda t: act.wait_ge(drained[second], (pr + i) * TT + t + 1))
                if not final:
                    act.wait_ge(gcol_ready, r + i * 2 + 2)
                    split_x(tb + 4 * i + 2, T_HIGH, gcol, xT_hi, i * 8 + 4)

            act.dma_start(cols[:], columns).then_inc(cols_loaded, 16)
            act.dma_start(lam_rows, lambdas.rearrange("(o a) d -> o a d", o=1).broadcast_to([P, 4, DK]))\
               .then_inc(lam_loaded, 16)
            act.wait_ge(cols_loaded, 16)
            for g in range(XG):
                high(g, g)
                split_x(TB_X1 + 2 * g, T_LOW if g % 2 == 0 else T_HIGH, cols[:, BT * g:BT * (g + 1)], xT_hi, BT * g)
            gate_up(CH_FFN1, PR_FFN1, TB_H1, 1, 0, first=True, start=True)
            with act.Fori(1, GROUPS) as c:
                gate_up(CH_FFN1, PR_FFN1, TB_H1, 1, c)
            split_hidden(TB_H1 + 2 * (GROUPS - 1), GROUPS - 1)
            with act.Fori(0, XG // 2) as i:
                residual(CH_DOWN1, PR_DOWN1, TB_XM, XG, 0, CF, False, i)

            act.wait_ge(lam_dots, 1)
            act.activation(lam_exp[:], lam_dot[:], ACT.Exp).then_inc(lam_exps, 1)
            act.wait_ge(rstd_ready, 2)
            with act.Fori(0, J) as j:
                ch, pair, hb, tb, jb = CH_MIX + 6 * CD * j, PR_MIX + 3 * j, HJ * j, TB_HEAD + HJ * j, 4 * j
                for u in (Q, K, V, B, C, X):
                    for k in range(CD):
                        if k == CD - 1 and u != X:
                            for t in range(TT):
                                unit_done(ch + CD * (u + 1), pair + u // 2, u % 2, t)
                                act.activation(part_s[u][:, t], bank[2 * (u % 2) + t][:], ACT.Copy,
                                               scale=rstd[:, t:t + 1]).then_inc(drained[u % 2], 1)
                        s = CD * (u - B) + k
                        for h in range(HJ):
                            n = hb + h + 1
                            if s == 5 * h + 5:
                                act.wait_ge(heads_ready, n)
                                for t in range(TT):
                                    a = act.activation(gate[:, t, 0:DV], bank[7][:, t * DV:(t + 1) * DV], ACT.Square,
                                                       accum_out=osq[:, t:t + 1])
                                a.then_inc(head_squares, 1)
                            if s == 5 * h + 7:
                                act.wait_ge(turned, tb + h + 1)
                                act.activation(yT_hi[:, bass.ds(j * HJ + (KD // 2 + h), 1), :].rearrange("p a n -> p (a n)"),
                                               bank[4][:, 0:SEQ], ACT.Copy, scale=sub_col[:, 0:1]).then_inc(turned_hi, 1)
                            if s == 5 * h:
                                act.wait_ge(qk_turned, n)
                                act.activation(qkT[:], bank[4][:], ACT.Copy).then_inc(qk_copied, 1)
                            if s == 5 * h + 2:
                                act.wait_ge(masked, n)
                                for c in range(2):
                                    for t in range(TT):
                                        e = probs[:, c, t * P:t * P + (t + 1) * P]
                                        m = 2 * c + t
                                        a = act.activation(e, e, ACT.Exp, bias=negmax[:, m:m + 1], scale=SCALE,
                                                           accum_out=rowsum[:, m:m + 1])
                                a.then_inc(exps_done, 1)
                            if s == 5 * h + 4:
                                act.wait_ge(attn_turned, n)
                                act.activation(attnT[:], bank[7][:, 0:3 * P], ACT.Copy).then_inc(attn_copied, 1)
                        high(ch + CD * u + k + RING, k % RING)
                        if s == 14:
                            for b in range(2):
                                act.wait_ge(conv_turned, jb + b + 1)
                                act.activation(bT[:, 2 * b:2 * b + 2, :], bank[5 + b][:].rearrange("p (a n) -> p a n", a=2),
                                               ACT.Copy).then_inc(conv_copied, 1)
                for b in range(2):
                    act.wait_ge(conv_turned, jb + b + 3)
                    act.activation(upad[:, 2 * b:2 * b + 2, 2:SEQ + 2], bank[5 + b][:].rearrange("p (a n) -> p a n", a=2),
                                   ACT.Copy).then_inc(conv_copied, 1)
                act.wait_ge(conv_ready, j + 1)
                act.activation(yT_hi[:, bass.ds(j * BT, BT), :], conv[:], ACT.Copy).then_inc(conv_hi, 1)
            with act.Fori(0, XG // 2) as i:
                residual(CH_OUT, PR_OUT, TB_X2, 2 * XG, XG, CD, False, i)

            gate_up(CH_FFN2, PR_FFN2, TB_H2, 3, 0, first=True)
            with act.Fori(1, GROUPS) as c:
                gate_up(CH_FFN2, PR_FFN2, TB_H2, 3, c)
            split_hidden(TB_H2 + 2 * (GROUPS - 1), GROUPS - 1)
            for i in range(XG // 2):
                residual(CH_DOWN2, PR_DOWN2, None, 3 * XG, 2 * XG, CF, True, i, last=(i == XG // 2 - 1))
            act.wait_ge(x_saved, 3 * XG + 1)
            act.wait_ge(rstd_ready, 4)
            for g in range(XG):
                cs = slice(g * W, (g + 1) * W)
                act.activation(x[:, 0, cs], x[:, 0, cs], ACT.Copy, scale=rstd[:, 0:1]).then_inc(scaled[0], 1)

        @block.vector
        def _(dve):
            steps = Steps(dve, vector_step)
            link = steps.link

            def low(m, slot):
                dve.wait_ge(hi_ready, m + 1)
                dve.tensor_tensor(w_lo[slot][:], raw[slot][:], w_hi[slot][:].bitcast(F32), ALU.subtract)\
                   .then_inc(lo_ready, 1)

            def split_x(tb, banks, gain, hi, lo, k0):
                for b in range(2):
                    dve.wait_ge(turned_hi, tb + b + 1)
                    for kk in range(2):
                        blk = 2 * b + kk
                        tile = bass.ds(k0 + blk, 1)
                        v = dve.scalar_tensor_tensor(
                            out=lo[:, tile, :].rearrange("p a n -> p (a n)"), in0=bank[banks[b]][:, kk * SEQ:(kk + 1) * SEQ],
                            scalar=gain[:, blk:blk + 1], in1=hi[:, tile, :].rearrange("p a n -> p (a n)").bitcast(F32),
                            op0=ALU.mult, op1=ALU.subtract)
                    v.then_inc(turned_lo, 1)

            def split_hidden(tb, c):
                for b in range(2):
                    dve.wait_ge(turned_hi, tb + b + 1)
                    tiles = bass.ds(BT * c + 2 * b, 2)
                    dve.tensor_tensor(hT_lo[:, tiles, :], bank[T_LOW[b]][:].rearrange("p (a n) -> p a n", a=2),
                                      hT_hi[:, tiles, :].bitcast(F32), ALU.subtract).then_inc(turned_lo, 1)

            def inverse_root(v_out, sums, y, width):
                link(dve.tensor_scalar(v_out, sums, 1.0 / width, EPS, ALU.mult, ALU.add))
                link(dve.tensor_scalar(y.bitcast(I32), v_out.bitcast(I32), 1, None, ALU.logical_shift_right))
                link(dve.tensor_scalar(y.bitcast(I32), y.bitcast(I32), -1.0, MAGIC, ALU.mult, ALU.add))
                for _ in range(NEWTON):
                    link(dve.tensor_tensor(nt[:], v_out, y, ALU.mult))
                    link(dve.scalar_tensor_tensor(out=nt[:], in0=nt[:], scalar=-0.5, in1=y, op0=ALU.mult, op1=ALU.mult))
                    link(dve.scalar_tensor_tensor(out=y, in0=nt[:], scalar=1.5, in1=y, op0=ALU.add, op1=ALU.mult))

            def add_squares(q):
                if not (isinstance(q, int) and q == 0):
                    dve.wait_ge(sums_taken, q)
                dve.wait_ge(squares_ready, q + 1)
                dve.tensor_tensor(ssum[:], ssum[:], sq[:], ALU.add).then_inc(sums_taken, 1)

            def norm_factor(groups_before, last=False):
                dve.wait_ge(sums_taken, groups_before)
                inverse_root(nv[:], ssum[:], rstd[:], D)
                dve.sem_inc(rstd_ready, 1)
                if not last:
                    link(dve.memset(ssum[:], 0.0))

            def unit_done(ch_end, pair, second, t):
                if t == 0:
                    dve.wait_ge(upper_done, pair * 2 + second + 1)
                else:
                    dve.wait_ge(chunk_used, ch_end)

            def gate_up(ch, pr, tbh, c, first=False, start=False):
                base = ch + 2 * CD * c
                for n in range(2 * CD):
                    if n == 2 * CD - 1:
                        if first and not start:
                            dve.wait_ge(x_saved, 2 * XG + 1)
                        dve.wait_ge(drained[0], (pr + c + 1) * TT)
                        for t in range(TT):
                            unit_done(base + 2 * CD, pr + c, 1, t)
                            dve.scalar_tensor_tensor(out=turn_in[:, t], in0=bank[2 + t][:], scalar=rstd[:, t:t + 1],
                                                     in1=gate[:, t], op0=ALU.mult, op1=ALU.mult).then_inc(drained[1], 1)
                    low(base + n + RING, n % RING)
                    if start and 2 <= n < 2 + XG:
                        add_squares(n - 2)
                        if n == 1 + XG:
                            norm_factor(XG)
                    if not first and n == 1:
                        split_hidden(tbh + 2 * (c - 1), c - 1)

            def residual(ch, pr, tb, q, r, chunks, factor, final, i, last=False):
                for second in range(2):
                    g = i * 2 + second
                    for k in range(chunks):
                        if k == chunks - 1:
                            dve.wait_ge(squares_ready, q + g)
                            dve.wait_ge(x_saved, r + g + 1)
                            for t in range(TT):
                                unit_done(ch + 2 * chunks * i + chunks * (second + 1), pr + i, second, t)
                                dve.scalar_tensor_tensor(out=turn_in[:, t], in0=bank[2 * second + t][:], scalar=factor,
                                                         in1=x[:, t, bass.ds(g * W, W)], op0=ALU.mult, op1=ALU.add)\
                                   .then_inc(drained[second], 1)
                        if not (last and second == 1 and k >= chunks - RING):
                            low(ch + 2 * chunks * i + chunks * second + k + RING, (chunks * second + k) % RING)
                        if second == 1 and k == 1:
                            if not final:
                                split_x(tb + 4 * i, T_HIGH, gcol, xT_hi, xT_lo, i * 8)
                    add_squares(q + g)
                if not final:
                    split_x(tb + 4 * i + 2, T_HIGH, gcol, xT_hi, xT_lo, i * 8 + 4)

            link(dve.memset(ssum[:], 0.0))
            dve.wait_ge(cols_loaded, 16)
            for g in range(XG):
                low(g, g)
                split_x(TB_X1 + 2 * g, T_LOW if g % 2 == 0 else T_HIGH, cols[:, BT * g:BT * (g + 1)], xT_hi, xT_lo, BT * g)
            dve.wait_ge(lam_loaded, 16)
            for n in range(2):
                link(dve.tensor_tensor_reduce(lam_rows[:, 2 * n], lam_rows[:, 2 * n], lam_rows[:, 2 * n + 1], 1.0, 0.0,
                                              ALU.mult, ALU.add, lam_dot[:, n:n + 1]))
            dve.sem_inc(lam_dots, 1)
            link(dve.tensor_scalar(sub_col[:], cols[:, COL_SUB:COL_SUB + 1], 1.0 - LAMBDA_INIT, None, ALU.mult))
            gate_up(CH_FFN1, PR_FFN1, TB_H1, 0, first=True, start=True)
            with dve.Fori(1, GROUPS) as c:
                gate_up(CH_FFN1, PR_FFN1, TB_H1, c)
            split_hidden(TB_H1 + 2 * (GROUPS - 1), GROUPS - 1)
            with dve.Fori(0, XG // 2) as i:
                residual(CH_DOWN1, PR_DOWN1, TB_XM, XG, 0, CF, 0.5, False, i)
            norm_factor(2 * XG)

            dve.memset(upad[:, :, 0:2], 0.0).then_inc(conv_free, 1)
            dve.wait_ge(lam_exps, 1)
            link(dve.tensor_tensor(neg_lam[:], lam_exp[:, 1:2], lam_exp[:, 0:1], ALU.subtract))
            link(dve.tensor_scalar(neg_lam[:], neg_lam[:], -LAMBDA_INIT, None, ALU.add))
            dve.wait_ge(mask_ready, 3)
            with dve.Fori(0, J) as j:
                steps.enter(j, HJ * (1 + 4 + 3 + 3 * NEWTON) + 4)
                ch, pair, hb, tb, jb = CH_MIX + 6 * CD * j, PR_MIX + 3 * j, HJ * j, TB_HEAD + HJ * j, 4 * j
                for u in (Q, K, V, B, C, X):
                    for k in range(CD):
                        if k == CD - 1 and u == X:
                            dve.wait_ge(drained[0], (pair + 3) * TT)
                            for t in range(TT):
                                unit_done(ch + CD * (u + 1), pair + 2, 1, t)
                                dve.scalar_tensor_tensor(out=part_s[C][:, t], in0=bank[2 + t][:], scalar=rstd[:, t:t + 1],
                                                         in1=part_s[C][:, t], op0=ALU.mult, op1=ALU.mult)\
                                   .then_inc(drained[1], 1)
                        s = CD * (u - B) + k
                        for h in range(HJ):
                            n = hb + h + 1
                            if s == 5 * h + 6:
                                dve.wait_ge(head_squares, n)
                                inverse_root(nv[:], osq[:], orstd[:], DV)
                                for t in range(TT):
                                    v = dve.tensor_scalar(head[:, t], bank[7][:, t * DV:(t + 1) * DV],
                                                          orstd[:, t:t + 1], None, ALU.mult)
                                v.then_inc(heads_scaled, 1)
                            if s == 5 * h + 7:
                                dve.wait_ge(turned_hi, tb + h + 1)
                                tile = bass.ds(j * HJ + (KD // 2 + h), 1)
                                dve.scalar_tensor_tensor(out=yT_lo[:, tile, :].rearrange("p a n -> p (a n)"),
                                                         in0=bank[4][:, 0:SEQ], scalar=sub_col[:, 0:1],
                                                         in1=yT_hi[:, tile, :].rearrange("p a n -> p (a n)").bitcast(F32),
                                                         op0=ALU.mult, op1=ALU.subtract).then_inc(turned_lo, 1)
                            if s == 5 * h + 1:
                                dve.wait_ge(scores_ready, n)
                                dve.memset(spare[:], 0.0)
                                for c in range(2):
                                    for t in range(TT):
                                        cs = slice(t * P, t * P + (t + 1) * P)
                                        v = dve.tensor_tensor_reduce(probs[:, c, cs], bank[5 + c][:, cs], mask[:, cs], 1.0,
                                                                     LOWEST, ALU.add, ALU.max, rowmax[:, 2 * c + t:2 * c + t + 1])
                                link(v)
                                dve.tensor_scalar(negmax[:], rowmax[:], -SCALE, None, ALU.mult).then_inc(masked, 1)
                            if s == 5 * h + 2:
                                dve.wait_ge(exps_done, n)
                                link(dve.reciprocal(rinv[:], rowsum[:]))
                                link(dve.tensor_scalar(rneg[:], rinv[:, 2:4], neg_lam[:, 0:1], None, ALU.mult))
                                for t in range(TT):
                                    cs = slice(t * P, t * P + (t + 1) * P)
                                    link(dve.tensor_scalar(attn[:, cs], probs[:, 0, cs], rinv[:, t:t + 1], None, ALU.mult))
                                for t in range(TT):
                                    cs = slice(t * P, t * P + (t + 1) * P)
                                    v = dve.scalar_tensor_tensor(out=attn[:, cs], in0=probs[:, 1, cs], scalar=rneg[:, t:t + 1],
                                                                 in1=attn[:, cs], op0=ALU.mult, op1=ALU.add)
                                v.then_inc(attn_ready, 1)
                        low(ch + CD * u + k + RING, k % RING)
                dve.wait_ge(cw_ready, j + 1)
                dve.wait_ge(conv_copied, jb + 4)
                for b in range(BT):
                    v = dve.tensor_scalar(conv[:, b], upad[:, b, 0:SEQ], cw[:, 0, b:b + 1], None, ALU.mult)
                link(v)
                for tap in (1, 2):
                    for b in range(BT):
                        v = dve.scalar_tensor_tensor(out=conv[:, b], in0=upad[:, b, tap:tap + SEQ], scalar=cw[:, tap, b:b + 1],
                                                     in1=conv[:, b], op0=ALU.mult, op1=ALU.add)
                    link(v)
                link(dve.tensor_tensor(conv[:], conv[:], bT[:], ALU.mult))
                dve.sem_inc(conv_ready, 1)
                dve.wait_ge(conv_hi, j + 1)
                dve.sem_inc(conv_free, 1)
                tiles = bass.ds(j * BT, BT)
                dve.tensor_tensor(yT_lo[:, tiles, :], conv[:], yT_hi[:, tiles, :].bitcast(F32), ALU.subtract)\
                   .then_inc(conv_lo, 1)
            steps.leave(J)
            with dve.Fori(0, XG // 2) as i:
                residual(CH_OUT, PR_OUT, TB_X2, 2 * XG, XG, CD, 1.0, False, i)
            norm_factor(3 * XG)

            gate_up(CH_FFN2, PR_FFN2, TB_H2, 0, first=True)
            with dve.Fori(1, GROUPS) as c:
                gate_up(CH_FFN2, PR_FFN2, TB_H2, c)
            split_hidden(TB_H2 + 2 * (GROUPS - 1), GROUPS - 1)
            for i in range(XG // 2):
                residual(CH_DOWN2, PR_DOWN2, None, 3 * XG, 2 * XG, CF, 0.5, True, i, last=(i == XG // 2 - 1))
            norm_factor(4 * XG, last=True)
            dve.wait_ge(x_saved, 3 * XG + 1)
            for g in range(XG):
                cs = slice(g * W, (g + 1) * W)
                dve.tensor_scalar(x[:, 1, cs], x[:, 1, cs], rstd[:, 1:2], None, ALU.mult).then_inc(scaled[1], 1)

        @block.gpsimd
        def _(pool):
            pool.memset(ident[:], 0.0).then_inc(ident_ready, 1)
            pool.wait_ge(ident_ready, 1)
            pool.affine_select(out=ident[:], in_=ident[:], compare_op=ALU.not_equal, fill=1.0, base=0,
                               pattern=[[-1, P]], channel_multiplier=1).then_inc(ident_ready, 1)
            pool.memset(mask[:], 0.0).then_inc(mask_ready, 1)
            pool.wait_ge(mask_ready, 1)
            for n, b in enumerate((0, 2)):
                m = mask[:, b * P:(b + 1) * P]
                pool.affine_select(out=m, in_=m, compare_op=ALU.is_ge, fill=MASKED, base=0,
                                   pattern=[[-1, P]], channel_multiplier=1).then_inc(mask_ready, 1)

            def save(pr, tb, r, gain, chunks):
                with pool.Fori(0, XG // 2) as i:
                    for second in range(2):
                        g = i * 2 + second
                        pool.wait_ge(turned_lo, tb + 4 * i + 2 * second)
                        pool.tensor_copy(gcol[:], cols[:, bass.ds(i * 8 + (gain + BT * second), BT)]).then_inc(gcol_ready, 1)
                        pool.wait_ge(drained[second], (pr + i + 1) * TT)
                        pool.tensor_copy(x[:, :, bass.ds(g * W, W)], turn_in[:]).then_inc(x_saved, 1)

            pool.dma_start(gfin[:], gf.rearrange("(a n) -> a n", a=1).broadcast_to([P, D])).then_inc(gfin_loaded, 16)
            pool.wait_ge(cols_loaded, 16)
            pool.sem_inc(x_saved, 1)
            save(PR_DOWN1, TB_XM, 0, COL_GM, CF)
            taps = cols[:, COL_CONV:COLS].rearrange("p (k a) -> p k a", k=3)
            with pool.Fori(0, J) as j:
                pool.wait_ge(conv_free, j + 1)
                pool.tensor_copy(cw[:], taps[:, :, bass.ds(j * BT, BT)]).then_inc(cw_ready, 1)
            save(PR_OUT, TB_X2, XG, COL_G2, CD)
            pool.wait_ge(gfin_loaded, 16)
            with pool.Fori(0, XG // 2) as i:
                for second in range(2):
                    g = i * 2 + second
                    pool.wait_ge(drained[second], (i + (PR_DOWN2 + 1)) * TT)
                    for t in range(TT):
                        p = pool.tensor_tensor(x[:, t, bass.ds(g * W, W)], turn_in[:, t], gfin[:, bass.ds(g * W, W)], ALU.mult)
                    p.then_inc(x_saved, 1)


def ring_count(m, slot):
    return (m - slot) * (16 // RING) + 16


_INS = ['x', 'ffn1_w_gate', 'ffn1_w_up', 'ffn1_w_down', 'w_in', 'w_out', 'ffn2_w_gate', 'ffn2_w_up', 'ffn2_w_down',
        'final_norm', 'columns', 'lambdas']
_OUTS = [((1, SEQ, D), 'float32')]


def kernel(**inputs):
    import numpy as _np
    import concourse.bacc as _bacc
    from concourse import mybir as _mybir
    from concourse.bass_utils import run_bass_kernel_spmd as _run

    rows = [_np.asarray(inputs[n]).reshape(-1, P) for n in ('ffn1_norm', 'mix_norm', 'ffn2_norm', 'subln_w', 'conv_w')]
    inputs = dict(inputs, columns=_np.concatenate(rows).T, lambdas=_np.concatenate(
        [_np.asarray(inputs[n]) for n in ('lambda_q1', 'lambda_k1', 'lambda_q2', 'lambda_k2')]))

    nc = _bacc.Bacc("TRN2", target_bir_lowering=False, num_devices=1)
    arrays, args = {}, []
    for name in _INS:
        a = _np.ascontiguousarray(inputs[name])
        arrays[f"in_{name}_dram"] = a
        args.append(nc.dram_tensor(f"in_{name}_dram", a.shape, _mybir.dt.from_np(a.dtype), kind="ExternalInput").ap())
    for i, (shape, dtype) in enumerate(_OUTS):
        dt = _mybir.dt.from_np(_np.dtype(dtype))
        args.append(nc.dram_tensor(f"out_{i}_dram", shape, dt, kind="ExternalOutput").ap())
    hybrid_block(nc, *args)
    r = _run(nc, [arrays], core_ids=[0])
    got = tuple(r.results[0][f"out_{i}_dram"] for i in range(len(_OUTS)))
    return got[0]
```
